# Optimizing a Trainium2 kernel written in Bass

```python
import jax, jax.numpy as jnp
from jax import lax
import numpy as np

D_MODEL = 1024
BATCH = 1
SEQ = 128
DEPTH = 1
DEC_BATCH = 1
DEC_SEQ = 1024
PAST_LEN = 128

GRID_W = 64
MIX_W = D_MODEL
GLA_W = MIX_W // 4
GLA_HEADS = 4
GLA_DK = GLA_W // GLA_HEADS
GLA_DV = GLA_W // GLA_HEADS
GLA_LR = 16
GLA_TAU = 16.0
GLA_CHUNK = 64
GMLP_W = MIX_W // 4
GMLP_GROUPS = 4
GMLP_CHUNK = 128
CONV_W = MIX_W // 4
FNET_W = MIX_W - GLA_W - GMLP_W - CONV_W
FNET_GROUPS = 4
IN_WIDTHS = (GLA_W, GLA_W, GLA_W, GLA_W, GLA_LR, GLA_LR, GMLP_W, GMLP_W, CONV_W, CONV_W, CONV_W, FNET_W)
IN_SPLITS = tuple(sum(IN_WIDTHS[:i + 1]) for i in range(len(IN_WIDTHS) - 1))
IN_W = sum(IN_WIDTHS)
N_EXPERTS = 64
TOP_K = 8
N_GROUPS = 8
TOPK_GROUPS = 4
EXPERTS_PER_GROUP = N_EXPERTS // N_GROUPS
EXPERT_FF = D_MODEL // 4
SHARED_FF = D_MODEL // 4
ROUTED_SCALE = 2.5
MOE_BLOCK = 128
DEEPNORM_ALPHA = (2 * DEPTH) ** 0.25
DEEPNORM_BETA = (8 * DEPTH) ** -0.25
LN_EPS = 1e-5
RMS_EPS = 1e-6
POS_BASE = 10000.0

kernel_name = "hybrid_gla_sgu_conv_fnet_moe_prefix_dit_step"

def layer_norm(x, g=None, b=None):
    xf = x.astype(jnp.float32)
    mu = jnp.mean(xf, axis=-1, keepdims=True)
    var = jnp.mean(jnp.square(xf - mu), axis=-1, keepdims=True)
    y = (xf - mu) * lax.rsqrt(var + LN_EPS)
    if g is not None:
        y = y * g.astype(jnp.float32) + b.astype(jnp.float32)
    return y.astype(x.dtype)

def grid_sincos(rows, d):
    quarter = d // 4
    omega = 1.0 / (POS_BASE ** (jnp.arange(quarter, dtype=jnp.float32) / quarter))
    r = jnp.repeat(jnp.arange(rows, dtype=jnp.float32), GRID_W)
    col = jnp.tile(jnp.arange(GRID_W, dtype=jnp.float32), rows)
    er = r[:, None] * omega
    ec = col[:, None] * omega
    return jnp.concatenate([jnp.sin(er), jnp.cos(er), jnp.sin(ec), jnp.cos(ec)], axis=-1)

def gla_chunked(q, k, v, log_a, s0):
    bsz, nh, n, dk = q.shape
    nc = n // GLA_CHUNK
    rs = lambda t: t.astype(jnp.float32).reshape(bsz, nh, nc, GLA_CHUNK, t.shape[-1])
    q, k, v, log_a = rs(q) * (dk ** -0.5), rs(k), rs(v), rs(log_a)
    b = jnp.cumsum(log_a, axis=3)
    b_last = b[:, :, :, -1:, :]
    q_dec = q * jnp.exp(b)
    k_inv = k * jnp.exp(-b)
    k_end = k * jnp.exp(b_last - b)
    mask = jnp.tril(jnp.ones((GLA_CHUNK, GLA_CHUNK), jnp.float32))
    attn = jnp.einsum('bhcld,bhcmd->bhclm', q_dec, k_inv) * mask
    o_intra = jnp.einsum('bhclm,bhcmv->bhclv', attn, v)
    chunk_kv = jnp.einsum('bhcld,bhclv->bhcdv', k_end, v)
    decay = jnp.exp(b_last[:, :, :, 0, :])

    def step(s, inp):
        qd, kv, dc = inp
        o = jnp.einsum('bhld,bhdv->bhlv', qd, s)
        return dc[..., None] * s + kv, o

    s_fin, o_inter = lax.scan(step, s0.astype(jnp.float32),
                              (jnp.moveaxis(q_dec, 2, 0), jnp.moveaxis(chunk_kv, 2, 0), jnp.moveaxis(decay, 2, 0)))
    o = o_intra + jnp.moveaxis(o_inter, 0, 2)
    return o.reshape(bsz, nh, n, -1), s_fin

def mixer(h, p, s0_fwd, s0_bwd):
    bsz, n, _ = h.shape
    proj = h @ p["w_in"]
    q, k, v, g_out, lr_f, lr_b, sg_u, sg_v, cv_b, cv_c, cv_x, ft = jnp.split(proj, IN_SPLITS, axis=-1)

    heads = lambda t: t.reshape(bsz, n, GLA_HEADS, -1).transpose(0, 2, 1, 3)
    flip = lambda t: jnp.flip(t, axis=2)
    log_a_f = jax.nn.log_sigmoid((lr_f @ p["w_gla_a"][0] + p["b_gla_a"][0]).astype(jnp.float32)) / GLA_TAU
    log_a_b = jax.nn.log_sigmoid((lr_b @ p["w_gla_a"][1] + p["b_gla_a"][1]).astype(jnp.float32)) / GLA_TAU
    qh, kh, vh = heads(q), heads(k), heads(v)
    o_f, s_f = gla_chunked(qh, kh, vh, heads(log_a_f), s0_fwd)
    o_b, s_b = gla_chunked(flip(qh), flip(kh), flip(vh), flip(heads(log_a_b)), s0_bwd)
    o = o_f + flip(o_b)
    o = o * lax.rsqrt(jnp.mean(jnp.square(o), axis=-1, keepdims=True) + RMS_EPS)
    o = o * p["gla_norm_g"].astype(jnp.float32).reshape(GLA_HEADS, 1, GLA_DV)
    y_gla = o.transpose(0, 2, 1, 3).reshape(bsz, n, GLA_W).astype(h.dtype) * jax.nn.silu(g_out)

    vn = layer_norm(sg_v, p["sgu_norm_g"], p["sgu_norm_b"])
    vn = vn.reshape(bsz, n // GMLP_CHUNK, GMLP_CHUNK, GMLP_GROUPS, -1)
    sp = jnp.einsum('gst,bctgd->bcsgd', p["w_sgu"], vn) + p["b_sgu"].T[:, :, None]
    y_sgu = sg_u * sp.reshape(bsz, n, GMLP_W)

    z = cv_c * cv_x
    zp = jnp.pad(z, ((0, 0), (1, 1), (0, 0)))
    wc = p["w_conv"]
    conv = wc[0] * zp[:, :-2] + wc[1] * zp[:, 1:-1] + wc[2] * zp[:, 2:]
    y_conv = cv_b * conv

    f = ft.reshape(bsz, n, FNET_GROUPS, -1).astype(jnp.float32)
    y_ft = jnp.fft.fft2(f, axes=(1, 3), norm="ortho").real.reshape(bsz, n, FNET_W).astype(h.dtype)

    y = jnp.concatenate([y_gla, y_sgu, y_conv, y_ft], axis=-1) @ p["w_out"]
    return y, s_f, s_b

def moe(h, p):
    bsz, n, d = h.shape
    x = h.reshape(-1, d)
    t = x.shape[0]
    scores = jax.nn.sigmoid((x @ p["w_router"]).astype(jnp.float32))
    biased = scores + p["router_bias"].astype(jnp.float32)
    grp_score = lax.top_k(biased.reshape(t, N_GROUPS, EXPERTS_PER_GROUP), 2)[0].sum(-1)
    _, top_g = lax.top_k(grp_score, TOPK_GROUPS)
    gmask = jnp.any(top_g[:, :, None] == jnp.arange(N_GROUPS)[None, None, :], axis=1)
    masked = jnp.where(jnp.repeat(gmask, EXPERTS_PER_GROUP, axis=1), biased, -jnp.inf)
    _, idx = lax.top_k(masked, TOP_K)
    w = jnp.take_along_axis(scores, idx, axis=1)
    w = w / jnp.sum(w, axis=-1, keepdims=True) * ROUTED_SCALE

    n_assign = t * TOP_K
    flat_e = idx.reshape(-1)
    order = jnp.argsort(flat_e)
    sorted_e = flat_e[order]
    tok = order // TOP_K
    w_sorted = w.reshape(-1)[order]
    counts = jnp.bincount(flat_e, length=N_EXPERTS)
    padded = ((counts + MOE_BLOCK - 1) // MOE_BLOCK) * MOE_BLOCK
    ends_padded = jnp.cumsum(padded)
    starts_padded = ends_padded - padded
    starts = jnp.cumsum(counts) - counts
    dest = starts_padded[sorted_e] + (jnp.arange(n_assign) - starts[sorted_e])
    n_blocks = -(-n_assign // MOE_BLOCK) + N_EXPERTS
    x_pad = jnp.zeros((n_blocks * MOE_BLOCK, d), x.dtype).at[dest].set(x[tok])
    block_expert = jnp.minimum(
        jnp.searchsorted(ends_padded, jnp.arange(n_blocks) * MOE_BLOCK, side='right'), N_EXPERTS - 1)

    def expert_block(args):
        xb, e = args
        return (jax.nn.silu(xb @ p["w_exp_gate"][e]) * (xb @ p["w_exp_up"][e])) @ p["w_exp_down"][e]

    y_blocks = lax.map(expert_block, (x_pad.reshape(n_blocks, MOE_BLOCK, d), block_expert))
    y_assign = y_blocks.reshape(-1, d)[dest] * w_sorted[:, None]
    routed = jax.ops.segment_sum(y_assign, tok, num_segments=t).astype(x.dtype)
    shared = (jax.nn.silu(x @ p["w_sh_gate"]) * (x @ p["w_sh_up"])) @ p["w_sh_down"]
    return (routed + shared).reshape(bsz, n, d)

def trunk_layer(x, cond, s0, p):
    mod = jax.nn.silu(cond) @ p["w_ada"] + p["b_ada"]
    sh1, sc1, g1, sh2, sc2, g2 = jnp.split(mod[:, None, :], 6, axis=-1)
    h = layer_norm(x) * (1 + sc1) + sh1
    y, s_f, s_b = mixer(h, p, s0[:, 0], s0[:, 1])
    x = layer_norm(DEEPNORM_ALPHA * x + g1 * y, p["ln1_g"], p["ln1_b"])
    h = layer_norm(x) * (1 + sc2) + sh2
    x = layer_norm(DEEPNORM_ALPHA * x + g2 * moe(h, p), p["ln2_g"], p["ln2_b"])
    return x, jnp.stack([s_f, s_b], axis=1)

def setup_inputs(seed: int = 0) -> dict:
    key = jax.random.key(seed)
    ks = iter(jax.random.split(key, 32))
    nrm = lambda shape, scale: scale * jax.random.normal(next(ks), shape, jnp.float32)
    L, D, E, F = DEPTH, D_MODEL, N_EXPERTS, EXPERT_FF
    return {
        "x_prompt": nrm((BATCH, SEQ, D), 1.0),
        "x_sample": nrm((DEC_BATCH, DEC_SEQ, D), 1.0),
        "c": nrm((DEC_BATCH, D), 1.0),
        "state_gla": nrm((DEC_BATCH, L, 2, GLA_HEADS, GLA_DK, GLA_DV), 0.5),
        "c_ctx": nrm((D,), 1.0),
        "w_ada": nrm((L, D, 6 * D), D ** -0.5),
        "b_ada": nrm((L, 6 * D), 0.02),
        "w_in": nrm((L, D, IN_W), D ** -0.5),
        "w_gla_a": nrm((L, 2, GLA_LR, GLA_W), GLA_LR ** -0.5),
        "b_gla_a": nrm((L, 2, GLA_W), 0.1),
        "gla_norm_g": 1.0 + nrm((L, GLA_W), 0.02),
        "sgu_norm_g": 1.0 + nrm((L, GMLP_W), 0.02),
        "sgu_norm_b": nrm((L, GMLP_W), 0.02),
        "w_sgu": nrm((L, GMLP_GROUPS, GMLP_CHUNK, GMLP_CHUNK), GMLP_CHUNK ** -0.5),
        "b_sgu": 1.0 + nrm((L, GMLP_GROUPS, GMLP_CHUNK), 0.02),
        "w_conv": nrm((L, 3, CONV_W), 3 ** -0.5),
        "w_out": nrm((L, MIX_W, D), DEEPNORM_BETA * MIX_W ** -0.5),
        "ln1_g": 1.0 + nrm((L, D), 0.02),
        "ln1_b": nrm((L, D), 0.02),
        "ln2_g": 1.0 + nrm((L, D), 0.02),
        "ln2_b": nrm((L, D), 0.02),
        "w_router": nrm((L, D, E), D ** -0.5),
        "router_bias": nrm((L, E), 0.01),
        "w_exp_gate": nrm((L, E, D, F), D ** -0.5),
        "w_exp_up": nrm((L, E, D, F), D ** -0.5),
        "w_exp_down": nrm((L, E, F, D), DEEPNORM_BETA * F ** -0.5),
        "w_sh_gate": nrm((L, D, SHARED_FF), D ** -0.5),
        "w_sh_up": nrm((L, D, SHARED_FF), D ** -0.5),
        "w_sh_down": nrm((L, SHARED_FF, D), DEEPNORM_BETA * SHARED_FF ** -0.5),
    }

def reference(x_prompt, x_sample, c, state_gla, c_ctx, w_ada, b_ada, w_in, w_gla_a, b_gla_a,
              gla_norm_g, sgu_norm_g, sgu_norm_b, w_sgu, b_sgu, w_conv, w_out,
              ln1_g, ln1_b, ln2_g, ln2_b, w_router, router_bias,
              w_exp_gate, w_exp_up, w_exp_down, w_sh_gate, w_sh_up, w_sh_down):
    def layer_params(l):
        return {
            "w_ada": w_ada[l], "b_ada": b_ada[l], "w_in": w_in[l],
            "w_gla_a": w_gla_a[l], "b_gla_a": b_gla_a[l], "gla_norm_g": gla_norm_g[l],
            "sgu_norm_g": sgu_norm_g[l], "sgu_norm_b": sgu_norm_b[l],
            "w_sgu": w_sgu[l], "b_sgu": b_sgu[l], "w_conv": w_conv[l], "w_out": w_out[l],
            "ln1_g": ln1_g[l], "ln1_b": ln1_b[l], "ln2_g": ln2_g[l], "ln2_b": ln2_b[l],
            "w_router": w_router[l], "router_bias": router_bias[l],
            "w_exp_gate": w_exp_gate[l], "w_exp_up": w_exp_up[l], "w_exp_down": w_exp_down[l],
            "w_sh_gate": w_sh_gate[l], "w_sh_up": w_sh_up[l], "w_sh_down": w_sh_down[l],
        }

    y_prompt = x_prompt
    s_zero = jnp.zeros((x_prompt.shape[0], 2, GLA_HEADS, GLA_DK, GLA_DV), jnp.float32)
    ctx_states = []
    for l in range(DEPTH):
        y_prompt, s_l = trunk_layer(y_prompt, c_ctx[None, :], s_zero, layer_params(l))
        ctx_states.append(s_l)
    new_state_gla = jnp.stack(ctx_states, axis=1).astype(x_prompt.dtype)

    rows = x_sample.shape[1] // GRID_W
    y_sample = x_sample + grid_sincos(rows, D_MODEL).astype(x_sample.dtype)[None]
    for l in range(DEPTH):
        y_sample, _ = trunk_layer(y_sample, c, state_gla[:, l], layer_params(l))

    return (y_prompt, y_sample, new_state_gla)


_drawn_inputs = setup_inputs


def setup_inputs(seed=0):
    import zlib

    import numpy as np

    out = dict(_drawn_inputs(seed))
    spreads = {}
    factors = {'state_gla': 8.0,
     'gla_norm_g': 3.606,
     'sgu_norm_g': 3.653,
     'sgu_norm_b': 2.931,
     'b_sgu': 2.733,
     'ln2_g': 2.833,
     'ln2_b': 2.949}
    for name, (base, spread) in spreads.items():
        noise = np.random.default_rng([zlib.crc32(name.encode()), seed]).standard_normal(out[name].shape)
        drawn = base * np.exp(spread * noise) if base else spread * noise
        out[name] = __import__('jax').numpy.asarray(drawn.astype(out[name].dtype))
    for name, factor in factors.items():
        out[name] = (out[name] * factor).astype(out[name].dtype)
    return out
```

```python
from contextlib import ExitStack

import concourse.bass as bass
import numpy as np
from concourse import mybir

F32 = mybir.dt.float32
BF16 = mybir.dt.bfloat16
I32 = mybir.dt.int32
ALU = mybir.AluOpType
ACT = mybir.ActivationFunctionType
AX = mybir.AxisListType.X

P = 128
D = 1024
KD = D // P
SAMPLE, PROMPT, GRID = 1024, 128, 64
T = SAMPLE + PROMPT
NT = T // P
ST = SAMPLE // P
GROUPS = [(0, 4), (4, 8), (8, 9)]
W = 256
HEADS, DK, CHUNK = 4, 64, 64
LR = 16
E, FF, TOPK, NGRP, TOPG = 64, 256, 8, 8, 4
NE = E + 1
ALPHA = 2.0 ** 0.25
LN_EPS, RMS_EPS = 1e-5, 1e-6
SCALE = 2.5
BIG = 1.0e30
NB = NT + (T * TOPK) // P + E
LOOK = 4
NBP = NB + 2 + LOOK + 1
PAIRS = (NB + 1) // 2
HX = D + NE + 15
NTRASH = P
SLOTS = 5
EW = 3 * D * FF // P

CONST = {}
_at = 0
for _n, _w in (("ident", P), ("cum", 2 * P), ("suf", 2 * P), ("mask", 4 * P), ("tri", P), ("tri64i", E), ("tri64s", E),
               ("low8", NGRP * NGRP), ("slot", P), ("blk", NBP), ("isroute", NBP), ("r0", NBP), ("tokid", NT), ("idcol", 3 * NT),
               ("trash", 1), ("negslot", 1), ("pastend", 1)):
    CONST[_n] = (_at, _w)
    _at += _w
NCONST = _at


def constants():
    c = np.zeros((P, NCONST), np.float32)
    p, q = np.arange(P)[:, None], np.arange(P)[None, :]

    def put(name, v):
        a, w = CONST[name]
        c[: v.shape[0], a:a + w] = v.reshape(v.shape[0], w)

    same = (p // CHUNK == q // CHUNK).astype(np.float32)
    put("ident", np.eye(P, dtype=np.float32))
    put("cum", np.concatenate([same * (p <= q), same * (p >= q)], 1) / 16)
    put("suf", np.concatenate([same * (p > q), same * (p < q)], 1) / 16)
    put("mask", np.concatenate([same * (p <= q)] * 2 + [same * (p >= q)] * 2, 1))
    put("tri", (p < q).astype(np.float32))
    e, f = np.arange(E)[:, None], np.arange(E)[None, :]
    put("tri64i", (e <= f).astype(np.float32))
    put("tri64s", (e < f).astype(np.float32))
    g = np.arange(NGRP)
    put("low8", np.tile((g[None, :] < g[:, None]).astype(np.float32).reshape(1, -1), (P, 1)))
    put("slot", np.tile(q, (P, 1)).astype(np.float32))
    b = np.arange(NBP)[None, :]
    put("blk", np.tile(b - NT, (P, 1)).astype(np.float32))
    put("isroute", np.tile(b >= NT, (P, 1)).astype(np.float32))
    put("r0", np.tile(np.where(b < NT, P * b, P * (b - NT)), (P, 1)).astype(np.float32))
    put("tokid", (np.arange(NT)[None, :] * P + p).astype(np.float32))
    ids = np.zeros((P, NT, 3), np.float32)
    ids[:, :, 0], ids[:, :, 1], ids[:, :, 2] = p, P * (np.arange(NT)[None, :] - NT), 1
    put("idcol", ids)
    put("trash", (T + p).astype(np.float32))
    past = np.zeros((E, 1), np.float32)
    past[-1] = -2.0 * NT
    put("pastend", past)
    put("negslot", (-p).astype(np.float32))
    return c


def position_tables():
    quarter = D // 4
    omega = (np.float32(1.0) / (np.float32(10000.0) ** (np.arange(quarter, dtype=np.float32) / np.float32(quarter)))).astype(np.float32)
    row = np.arange(SAMPLE // GRID, dtype=np.float32)[:, None] * omega
    col = np.arange(GRID, dtype=np.float32)[:, None] * omega
    two = lambda x: np.concatenate([np.sin(x.astype(np.float64)), np.cos(x.astype(np.float64))], 1).astype(np.float32)
    return two(row), two(col)


def dft_tables():
    u = np.arange(64)
    ang = 2 * np.pi * np.outer(u, u) / 64
    eye2 = np.eye(2)
    c, s = np.kron(eye2, np.cos(ang)), np.kron(eye2, np.sin(ang))
    feat = np.concatenate([c, -s, s, c, -s, -c], 1)
    b, k = np.arange(P)[:, None], np.arange(P)[None, :]
    tok = []
    for fn in (np.cos, np.sin):
        for d in range(ST):
            tok.append(fn(2 * np.pi * ((b * (ST * k + d)) % SAMPLE) / SAMPLE) / np.sqrt(SAMPLE * 64))
        tok.append(fn(2 * np.pi * ((b * k) % PROMPT) / PROMPT) / np.sqrt(PROMPT * 64))
    return feat.astype(np.float32), np.concatenate(tok, 1).astype(np.float32)


def build(nc, A, out_prompt, out_sample, out_state, stage=9, dbg=None):
    ctx = ExitStack()
    with ctx:
        sb = lambda n, s, d=F32: ctx.enter_context(nc.sbuf_tensor(n, s, d))
        sem = lambda n: ctx.enter_context(nc.semaphore(n))

        x0_dram = nc.dram_tensor("x0_dram", [T, D], F32).ap()
        x1_dram = nc.dram_tensor("x1_dram", [T, D], F32).ap()
        hx_dram = nc.dram_tensor("hx_dram", [T + NTRASH, HX], F32).ap()
        acc_dram = nc.dram_tensor("acc_dram", [T + NTRASH, D], F32).ap()

        R01 = sb("R01", [P, 3 * EW + KD * T + KD * D])
        R0 = R01[:, 0:3 * EW]
        R1 = R01[:, 3 * EW:]
        R2 = sb("R2", [P, 11 * T])
        const = sb("const", [P, NCONST])
        C = {n: const[:, a:a + w] for n, (a, w) in CONST.items()}
        ident = C["ident"]

        def carve(region, at, *shape, parts=P):
            n = int(np.prod(shape))
            v = region[0:parts, at:at + n]
            if len(shape) == 2:
                v = v.rearrange("p (a b) -> p a b", a=shape[0])
            elif len(shape) == 3:
                v = v.rearrange("p (a b c) -> p a b c", a=shape[0], b=shape[1])
            elif len(shape) == 4:
                v = v.rearrange("p (a b c d) -> p a b c d", a=shape[0], b=shape[1], c=shape[2])
            return v

        hT = carve(R0, 0, KD, T)
        RING = 4
        ring = carve(R0, KD * T, RING, KD, W)
        fr = carve(R0, 0, 8, 2, P)
        bs, bm = carve(R0, 2048, 2, 4, P), carve(R0, 3072, 2, 4, P)
        bpq, buv = carve(R0, 4096, 2, 2, P), carve(R0, 4608, 2, 2, P)
        uv = carve(R0, 5120, 2, 512)
        dft_f = carve(R0, 6144, 3, 256)
        dft_t = carve(R0, 6144 + 768, 2, 9, P)
        G0 = EW
        na = carve(R0, G0, 512)
        la = carve(R0, G0 + 512, 2, 512)
        e1 = carve(R0, G0 + 1536, 2, 4, P)
        ki = carve(R0, G0 + 2560, 2, 4, P)
        ke = carve(R0, G0 + 3584, 2, 512)
        qd = carve(R0, G0 + 4608, 3, 4, P)
        vt = carve(R0, G0 + 6144, 3, 512)
        am = carve(R0, G0 + 7680, 4, 512)
        am = am.rearrange("p (r h) x -> p r h x", r=2)
        S = carve(R0, G0 + 9728, 5, 4, P)
        osq = carve(R0, G0, NT * 256)
        yT = carve(R1, 0, KD, T)
        w_out = carve(R1, KD * T, KD, D)
        xn = carve(R1, 0, 2, 4, D)
        WO = KD * T
        xin = carve(R1, WO, 2, D)
        prow = carve(R1, WO + 2048, 2, 512)
        pcol = carve(R1, WO + 3072, 512)
        ZW = T + 4
        zc, zx, zt = carve(R1, WO, 2, ZW), carve(R1, WO + 2 * ZW, 2, ZW), carve(R1, WO + 4 * ZW, ZW)
        wsgu = carve(R1, WO + 5 * ZW, 4, P)
        vn = carve(R1, WO + 5 * ZW + 512, 2, W)
        qT, kT, vT, sgvT, ftT = (carve(R2, 2 * i * T, 2, T) for i in range(5))
        lrT = carve(R2, 10 * T, T)
        o_tm = carve(R2, 6 * T, NT, W)

        wgla = sb("wgla", [33, 512])
        wsguT = sb("wsguT", [P, 4, P])
        bsgu = sb("bsgu", [P, 2, P])
        sgu_gb = sb("sgu_gb", [P, 2, W])
        cond_rows = wsguT[0:16, 0, :]
        bada_rows = wsguT[0:48, 1, :]
        small = sb("small", [P, 640])
        cs = small[:, 0:16].rearrange("p (c j) -> p c j", c=2)
        badaT = small[:, 16:64]
        modT = small[:, 64:160].rearrange("p (m c) -> p m c", c=2)
        scp = small[:, 160:176].rearrange("p (m c) -> p m c", c=2)
        scp2 = small[:, 176:192].rearrange("p (m c) -> p m c", c=2)
        gng = small[:, 192:194]
        wcv = small[:, 194:200].rearrange("p (w j) -> p w j", w=3)
        st6 = small[:, 200:212].rearrange("p (a s) -> p a s", a=2)
        mv = small[:, 212:216].rearrange("p (r s) -> p r s", r=2)
        ivar = small[:, 216:218]
        rstd = small[:, 218:220]
        ones = small[:, 220:221]
        rms = small[:, 222:258]

        ps = ctx.enter_context(nc.psum_tensor("ps", [P, 8, 512], F32))

        const_in = sem("const_in")
        cond_in = sem("cond_in")
        gate_in = sem("gate_in")
        x_in = [sem(f"x_in{i}") for i in range(2)]
        x0_out = [sem(f"x0_out{i}") for i in range(2)]
        w_in = [sem(f"w_in{i}") for i in range(RING)]
        w_used = sem("w_used")
        cond_t, cs_ready, bada_ready = sem("cond_t"), sem("cs_ready"), sem("bada_ready")
        ada_mm, mod_ready = sem("ada_mm"), sem("mod_ready")
        x0_ready, xn_ready = sem("x0_ready"), sem("xn_ready")
        ivar_ready, rstd_ready = sem("ivar_ready"), sem("rstd_ready")
        dve_step, act_step, pool_step = sem("dve_step"), sem("act_step"), sem("pool_step")
        ring_mm, evac = sem("ring_mm"), sem("evac")
        pads, conv_done = sem("pads"), sem("conv_done")
        sgu_wt, sgu_wt_ready, sgv_t, vn_raw, vn_ready, sp_mm, sgu_done = (sem(n) for n in (
            "sgu_wt", "sgu_wt_ready", "sgv_t", "vn_raw", "vn_ready", "sp_mm", "sgu_done"))
        sgu_in = sem("sgu_in")
        dft_in, fr_ready, uv_mm, uv_ready, ft_mm, ft_done = (sem(n) for n in (
            "dft_in", "fr_ready", "uv_mm", "uv_ready", "ft_mm", "ft_done"))
        s_zero, s_init = sem("s_zero"), sem("s_init")
        (logit_mm, ln_ready, la_ready, bg_mm, e_ready, kv_t, v_ready, qk_ready, attn_mm, kv_mm, am_ready,
         S_ready, o_mm, o_acc, o_ready, o_t, gla_done) = (sem(n) for n in (
             "logit_mm", "ln_ready", "la_ready", "bg_mm", "e_ready", "kv_t", "v_ready", "qk_ready",
             "attn_mm", "kv_mm", "am_ready", "S_ready", "o_mm", "o_acc", "o_ready", "o_t", "gla_done"))
        state_out = sem("state_out")
        dbg_out = sem("dbg_out")

        w_ada_v = A["w_ada"][0].rearrange("(j p) n -> p j n", p=P)
        w_in_v = A["w_in"][0].rearrange("(j p) n -> p j n", p=P)
        COL = {}
        at = 0
        for n, w in (("q", W), ("k", W), ("v", W), ("go", W), ("lr", 2 * LR), ("sgu", W), ("sgv", W), ("cvb", W),
                     ("cvc", W), ("cvx", W), ("ft", W)):
            COL[n] = (at, w)
            at += w
        ADA1, ADA2 = 2 * D // W, 4 * D // W
        PROJ = ["cvc", "cvx", "cvb", "lr", "q", "k", "v", "sgv", "ft", "sgu", "go"]
        STREAM = [(w_ada_v, i * W, W) for i in range(ADA1)] + [(w_in_v, *COL[n]) for n in PROJ] \
            + [(w_ada_v, (ADA1 + i) * W, W) for i in range(ADA2)]
        HT_EV = KD * len(GROUPS)
        ev_after = {}
        r = HT_EV
        for n in PROJ:
            r += 3 * max(1, COL[n][1] // P)
            ev_after[n] = r
        EV_ALL = r
        DEST = {"q": qT, "k": kT, "v": vT, "sgv": sgvT, "ft": ftT, "cvb": yT[:, 4:6, :], "sgu": yT[:, 2:4, :],
                "go": yT[:, 0:2, :]}

        def ft_tile(u, d):
            return ST if u == ST else (u if d == 0 else ST - 1 - u)

        tile = lambda i: slice(i * P, (i + 1) * P)
        block = ctx.enter_context(nc.Block())

        def dft_terms(d):
            return {0: [(0, 0)], 4: [(1, 0)], 2: [(2, 0), (3, 2)], 6: [(2, 0), (3, 1)], 1: [(4, 0), (5, 2)],
                    7: [(4, 0), (5, 1)], 3: [(6, 0), (7, 1)], 5: [(6, 0), (7, 2)]}[d]

        g1_row, sc2_row, sh2_row = (carve(R2, 2 * D * i, 2, D) for i in range(3))
        ln1_row = carve(R2, 6 * D, 2, D)
        x1 = carve(R2, 8 * D, 2, D)
        h2T = carve(R2, 10 * D, 2, KD, P)
        x0 = carve(R0, EW, 2, D)
        h2n = carve(R0, EW + 2 * D, 2, D)
        h2 = carve(R0, EW + 4 * D, 2, D)
        w_router = carve(R0, 2 * EW, KD, E)
        rt = 2 * EW + KD * E
        N9 = NT * E
        scores, biased, rbuf, rbuf2, sel = (carve(R0, rt + i * N9, NT, E) for i in range(5))
        rt += 5 * N9
        rbias = carve(R0, rt, E)
        gm1, gm2, gcnt, gsum, gtmp = (carve(R0, rt + E + i * NT * NGRP, NT * NGRP) for i in range(5))
        rt += E + 5 * NT * NGRP
        top8 = carve(R0, rt, 2, 8)
        den = carve(R0, rt + 16, NT)
        wrow = carve(R0, rt + 32, NT, HX - D)
        cnt_i, cnt_f = R0[0:E, rt + 760:rt + 761].bitcast(I32), R0[0:E, rt + 761:rt + 762]
        endc = R0[0:E, rt + 762:rt + 763]
        nb_bc = R0[0:E, rt + 768:rt + 768 + P]
        cmp_b = R0[0:E, EW:EW + NBP]
        sel_b = carve(R0, EW + 512, N9 // 2).bitcast(BF16).rearrange("p (i e) -> p i e", i=NT)
        tri_b = carve(R0, EW + 1024, P // 2).bitcast(BF16)
        ones_b = carve(R0, EW + 1088, P // 2).bitcast(BF16)
        assert rt + 768 + P <= 3 * EW

        wexp = R01[:, 0:SLOTS * EW].rearrange("p (s w) -> p s w", s=SLOTS)
        B0 = 2 * EW
        xg = carve(R1, B0, 2, HX)
        h_sb = carve(R1, B0 + 2 * HX, 2, FF)
        hTe = carve(R1, B0 + 2 * HX + 512, 2, 2, P)
        sg = carve(R1, B0 + 2 * HX + 1024, 2, FF)
        xT = carve(R2, 0, 2, KD, P)
        yb = carve(R2, 2048, 2, D)
        g2_row = carve(R2, 4096, 2, D)
        ln2_row = carve(R2, 6144, 2, D)
        keytab = carve(R2, 8192, NT, NE)
        r0tab = carve(R2, 8192 + 600, NBP)
        hot = carve(R2, 9000, 2, NT * P // 2).bitcast(BF16).rearrange("p r (i s) -> p r i s", i=NT)
        idcol_b = carve(R2, 10200, 16).bitcast(BF16)[:, 0:3 * NT].rearrange("p (i c) -> p i c", i=NT)
        rc = carve(R2, 10220, 2, 16)
        lst = carve(R2, 10256, 4)
        gidx = carve(R2, 10260, 2).bitcast(I32)
        sidx = carve(R2, 10262, 2).bitcast(I32)
        wcol = carve(R2, 10264, 4)
        idxtab = carve(R2, 10272, NBP).bitcast(I32)
        etab = carve(R2, 10432, NBP, parts=1).bitcast(I32)
        endtab = carve(R2, 10592, NE, parts=1).bitcast(I32)
        etmp = carve(R2, 10660, NBP, parts=1)
        assert SLOTS * EW == 3 * EW + B0 and B0 + 2 * HX + 1536 <= KD * T + KD * D
        FR = 3
        acc_t, x1_t = carve(R0, 0, FR, D), carve(R0, FR * D, FR, D)

        (wout_in, row_in, x0r_in0, x0r_in1, row_mm, row_ready, w3_mm, y3_used, xa_raw, x1_ready, h2_ready,
         h2_t, h2T_ready, router_mm, score_ready, router_in, x1_out0, x1_out1, h2_out0, h2_out1) = (sem(n) for n in (
             "wout_in", "row_in", "x0r_in0", "x0r_in1", "row_mm", "row_ready", "w3_mm", "y3_used", "xa_raw", "x1_ready",
             "h2_ready", "h2_t", "h2T_ready", "router_mm", "score_ready", "router_in", "x1_out0", "x1_out1", "h2_out0",
             "h2_out1"))
        x0r_in, x1_out, h2_out = (x0r_in0, x0r_in1), (x1_out0, x1_out1), (h2_out0, h2_out1)
        (sel_ready, rank_mm, nb_ready, end_mm, cmp_ready, blk_mm, tables_ready, wrow_ready, wrow_out, zero_out,
         g2_mm, g2_ready, ln2_in) = (sem(n) for n in (
             "sel_ready", "rank_mm", "nb_ready", "end_mm", "cmp_ready", "blk_mm", "tables_ready", "wrow_ready", "wrow_out",
             "zero_out", "g2_mm", "g2_ready", "ln2_in"))
        ex_in = [sem(f"ex_in{i}") for i in range(SLOTS)]
        experts_ready = sem("experts_ready")
        xg_in = [sem(f"xg_in{i}") for i in range(2)]
        (hot_ready, list_mm, idx_ready, x_t, xT_ready, gu_mm, sg_ready, h_ready, ht_mm, hT_ready, y_mm, y_ready, y_out,
         wcol_ready, sidx_ready, moe_done, blk_step, gathers, scatters, sums_done) = (sem(n) for n in (
             "hot_ready", "list_mm", "idx_ready", "x_t", "xT_ready", "gu_mm", "sg_ready", "h_ready", "ht_mm", "hT_ready",
             "y_mm", "y_ready", "y_out", "wcol_ready", "sidx_ready", "moe_done", "blk_step", "gathers", "scatters", "sums_done"))
        fin_in = [sem(f"fin_in{i}") for i in range(FR)]
        fin_out = [sem(f"fin_out{i}") for i in range(FR)]
        t_ready, fin_raw, fin_ready = sem("t_ready"), sem("fin_raw"), sem("fin_ready")
        PRIME = 2
        cond_of = lambda i: 0 if i < ST else 1

        def at_least(eng, s, value):
            if not isinstance(value, int) or value > 0:
                eng.wait_ge(s, value)

        def block_steps(eng, step):
            for n in range(-LOOK - 1, 0):
                step(n, n)
            total = eng.value_load(endtab[0:1, NE - 1:NE], min_val=NT + E, max_val=NB)
            with eng.Fori(0, PAIRS) as i:
                with eng.If(2 * i < total):
                    for p in range(2):
                        step(2 * i + p, p)

        def expert_of(eng, b):
            return eng.value_load(etab[0:1, bass.ds(b, 1)], min_val=0, max_val=E)

        def load_expert(sp, slot, gate, up, down):
            sp.dma_start(wexp[:, slot, 0:2048], gate.rearrange("(p j) n -> p (j n)", p=P)).then_inc(ex_in[slot], 16)
            sp.dma_start(wexp[:, slot, 2048:4096], up.rearrange("(p j) n -> p (j n)", p=P)).then_inc(ex_in[slot], 16)
            sp.dma_start(wexp[:, slot, 4096:EW], down.rearrange("(p j) n -> p (j n)", p=P)).then_inc(ex_in[slot], 16)

        def phase3_sync(sp):
            sp.wait_ge(ft_done, 1)
            load_expert(sp, 0, A["w_sh_gate"][0], A["w_sh_up"][0], A["w_sh_down"][0])
            sp.wait_ge(gla_done, 6)
            sp.dma_start(w_router, A["w_router"][0].rearrange("(p j) n -> p j n", p=P)).then_inc(router_in, 16)
            sp.dma_start(rbias, A["router_bias"][0].partition_broadcast(P)).then_inc(router_in, 16)
            for k, n in enumerate(("ln1_g", "ln1_b")):
                sp.dma_start(ln1_row[:, k, :], A[n][0].partition_broadcast(P)).then_inc(row_in, 16)
            for i in range(NT):
                if i >= 2:
                    sp.wait_ge(xa_raw, i - 1)
                sp.dma_start(x0[:, i % 2, :], x0_dram[tile(i), :]).then_inc(x0r_in[i % 2], 16)
                if i >= 2:
                    sp.wait_ge(h2_ready, i - 1)
                    sp.dma_start(hx_dram[tile(i - 2), 0:D], h2[:, i % 2, :]).then_inc(h2_out[i % 2], 16)
            for i in range(NT, NT + 2):
                sp.wait_ge(h2_ready, i - 1)
                sp.dma_start(hx_dram[tile(i - 2), 0:D], h2[:, i % 2, :]).then_inc(h2_out[i % 2], 16)
            sp.wait_ge(w3_mm, NT)
            for s in (3, 4):
                load_expert(sp, s, *(A[f"w_exp_{n}"][0, s - 1] for n in ("gate", "up", "down")))
            sp.wait_ge(h2_out[0], 16 * 5)
            sp.wait_ge(h2_out[1], 16 * 4)
            sp.wait_ge(wrow_ready, 1)
            sp.dma_start(hx_dram[0:T, D:HX].rearrange("(i p) e -> p i e", p=P), wrow).then_inc(wrow_out, 16)
            for k, n in enumerate(("ln2_g", "ln2_b")):
                sp.dma_start(ln2_row[:, k, :], A[n][0].partition_broadcast(P)).then_inc(ln2_in, 16)
            sp.wait_ge(tables_ready, 1)
            sp.wait_ge(wrow_out, 16)
            for s in (1, 2):
                load_expert(sp, s, *(A[f"w_exp_{n}"][0, s - 1] for n in ("gate", "up", "down")))

            def publish(slot, uses):
                sp.wait_ge(ex_in[slot], 48 * uses)
                sp.nop().then_inc(experts_ready, 1)

            for s in range(SLOTS - 1):
                publish(s, 1)
            with sp.Fori(1, NE // SLOTS) as m:
                for s in range(SLOTS):
                    end = sp.value_load(endtab[0:1, bass.ds(SLOTS * m + s - SLOTS, 1)], min_val=NT, max_val=NB)
                    sp.wait_ge(y_mm, end)
                    load_expert(sp, s, *(A[f"w_exp_{n}"][0, bass.ds(SLOTS * m + s - 1, 1)].rearrange("o a b -> (o a) b")
                                         for n in ("gate", "up", "down")))
                    publish((s - 1) % SLOTS, m if s == 0 else m + 1)
            publish(SLOTS - 1, NE // SLOTS)
            sp.wait_ge(moe_done, 1)

            def store(i):
                sp.wait_ge(fin_ready, i + 1)
                dst = out_sample[0, tile(i), :] if i < ST else out_prompt[0]
                sp.dma_start(dst, acc_t[:, i % FR, :]).then_inc(fin_out[i % FR], 16)

            for i in range(NT):
                if i >= FR:
                    store(i - FR)
                    sp.wait_ge(fin_out[i % FR], 16 * (i // FR))
                sp.dma_start(acc_t[:, i % FR, :], acc_dram[tile(i), :]).then_inc(fin_in[i % FR], 16)
                sp.dma_start(x1_t[:, i % FR, :], x1_dram[tile(i), :]).then_inc(fin_in[i % FR], 16)
            for i in range(NT - FR, NT):
                store(i)
            for s in range(FR):
                sp.wait_ge(fin_out[s], 16 * (NT // FR))

        def phase3_pool(pool, done):
            tt = pool.tensor_tensor
            zero = S[:, 4].rearrange("p a b -> p (a b)")
            pool.dma_start(acc_dram.rearrange("(p a) (h x) -> p (a h) x", p=P, h=2),
                           zero.unsqueeze(1).to_broadcast((P, 2 * (T + NTRASH) // P, 512))).then_inc(zero_out, 16)
            pool.dma_start(hx_dram[T:T + NTRASH, 0:D].rearrange("p (h x) -> p h x", h=2),
                           zero.unsqueeze(1).to_broadcast((P, 2, 512))).then_inc(zero_out, 16)
            pool.dma_start(hx_dram[T:T + NTRASH, D:HX], zero[:, 0:HX - D]).then_inc(zero_out, 16)
            pool.wait_ge(zero_out, 48)
            pool.wait_ge(row_in, 32)
            pool.nop().then_inc(s_zero, 1)
            for i in range(NT):
                pool.wait_ge(xa_raw, i + 1)
                x = x1[:, i % 2, :]
                done(tt(x, x, ln1_row[:, 0, :], ALU.mult))
                tt(x, x, ln1_row[:, 1, :], ALU.add).then_inc(x1_ready, 1)
                pool.wait_ge(x1_ready, i + 1)
                pool.dma_start(x1_dram[tile(i), :], x).then_inc(x1_out[i % 2], 16)
            pool.wait_ge(x1_out[0], 16 * 5)
            pool.wait_ge(x1_out[1], 16 * 4)
            pool.wait_ge(tables_ready, 1)
            pool.wait_ge(wrow_out, 16)
            pool.nop().then_inc(sums_done, PRIME)

            def step(n, p):
                b = n + 4
                if not isinstance(n, int) or b >= 0:
                    at_least(pool, x_t, n + 3)
                    at_least(pool, wcol_ready, n + 3)
                    pool.wait_ge(idx_ready, n + 5)
                    pool.sem_inc(gathers)
                    pool.indirect_dma_start(out=xg[:, p % 2, :], out_offset=None, in_=hx_dram, in_offset=bass.
                                            IndirectOffsetOnAxis(ap=gidx[:, p % 2:p % 2 + 1], axis=0))\
                        .then_inc(xg_in[p % 2], 16)
                if not isinstance(n, int):
                    pool.wait_ge(y_ready, n + 1 + PRIME)
                    pool.wait_ge(sidx_ready, n + 1)
                    pool.sem_inc(scatters)
                    pool.indirect_dma_start(out=acc_dram, out_offset=bass.IndirectOffsetOnAxis(
                        ap=sidx[:, p:p + 1], axis=0), in_=yb[:, p, :], in_offset=None, compute_op=ALU.add).then_inc(y_out, 16)
                    pool.wait_ge(y_out, 16 * n + 16)
                    pool.sem_inc(sums_done)

            block_steps(pool, step)
            pool.nop().then_inc(moe_done, 1)
            for i in range(NT):
                pool.wait_ge(fin_raw, i + 1)
                x = acc_t[:, i % FR, :]
                tt(x, x, ln2_row[:, 0, :], ALU.mult).then_inc(t_ready, 1)
                pool.wait_ge(t_ready, i + 1)
                tt(x, x, ln2_row[:, 1, :], ALU.add).then_inc(fin_ready, 1)

        def rows_act(act, dst, groups, mm_sem, out_sem, banks=2, base=0):
            for k in range(groups):
                act.wait_ge(mm_sem, k + 1)
                act.activation(dst(k), ps[:, base + k % banks, :], ACT.Copy).then_inc(out_sem, 1)

        ROWS = [(g1_row, 16), (sh2_row, 24), (sc2_row, 32)]

        def phase3_act(act, inv_std):
            a = act.activation
            rows_act(act, lambda k: ROWS[k // 4][0][:, (k // 2) % 2, (k % 2) * 512:(k % 2 + 1) * 512], 12, row_mm, row_ready)
            k = 2 * NT + 1
            for s in range(NT + 2):
                for i in (s, s - 1):
                    if 0 <= i < NT:
                        inv_std(k)
                        k += 1
                i = s - 2
                if 0 <= i < NT:
                    act.wait_ge(h2_t, i + 1)
                    if i >= 2:
                        act.wait_ge(router_mm, i - 1)
                    a(h2T[:, i % 2].rearrange("p j t -> p (j t)").rearrange("p (h x) -> p h x", h=2), ps[:, 4:6, :], ACT.Copy)\
                        .then_inc(h2T_ready, 1)
            act.wait_ge(router_mm, NT)
            a(scores[:, 0:ST, :], ps[:, 6, :].rearrange("p (i e) -> p i e", e=E), ACT.Sigmoid)
            a(scores[:, ST, :], ps[:, 7, 0:E], ACT.Sigmoid).then_inc(score_ready, 1)
            rows_act(act, lambda k: g2_row[:, k // 2, (k % 2) * 512:(k % 2 + 1) * 512], 4, g2_mm, g2_ready, base=4)
            act.nop().then_inc(y_ready, PRIME)

            def step(n, p):
                dyn = not isinstance(n, int)
                p %= 2
                if dyn:
                    act.wait_ge(ht_mm, n + 1)
                    act.wait_ge(g2_ready, 4)
                    a(hTe[:, p].rearrange("p a b -> p (a b)"), ps[:, 6, 0:FF], ACT.Copy).then_inc(hT_ready, 1)
                if dyn or n + 2 >= 0:
                    at_least(act, gu_mm, n + 1)
                    act.wait_ge(x_t, n + 3)
                    act.wait_ge(g2_ready, 4)
                    a(xT[:, p].rearrange("p j t -> p (j t)").rearrange("p (h x) -> p h x", h=2), ps[:, 0:2, :], ACT.Copy)\
                        .then_inc(xT_ready, 1)
                if dyn or n + 1 >= 0:
                    act.wait_ge(gu_mm, n + 2)
                    act.wait_ge(g2_ready, 4)
                    a(sg[:, 1 - p, :], ps[:, 2 + (1 - p), 0:FF], ACT.Silu).then_inc(sg_ready, 1)
                if dyn:
                    act.wait_ge(y_mm, n + 1)
                    act.wait_ge(wcol_ready, n + 1)
                    act.wait_ge(sums_done, n + 1)
                    w = act.snap(n % 4)
                    act.wait_ge(g2_ready, 4)
                    a(yb[:, p, :].rearrange("p (h x) -> p h x", h=2), ps[:, 4:6, :], ACT.Copy,
                      scale=wcol[:, bass.ds(w, 1)]).then_inc(y_ready, 1)

            block_steps(act, step)
            for i in range(NT):
                inv_std(k)
                k += 1

        def phase3_pe(pe):
            mm = pe.matmul

            def rows(src, k, bank, mm_sem):
                for m in range(4):
                    v = src(m)
                    last = mm(ps[:, bank, m * P:(m + 1) * P], v.to_broadcast((P, P)), ident, start=True, stop=True)
                last.then_inc(mm_sem, 1)

            pe.wait_ge(gla_done, 6)
            for k in range(12):
                base, c, half = ROWS[k // 4][1], (k // 2) % 2, k % 2
                if k >= 2:
                    pe.wait_ge(row_ready, k - 1)
                if base == 32:
                    rows(lambda m: scp2[:, 4 * half + m, c:c + 1], k, k % 2, row_mm)
                else:
                    rows(lambda m: modT[:, base + 4 * half + m, c:c + 1], k, k % 2, row_mm)
            pe.wait_ge(wout_in, 16)
            pe.wait_ge(row_ready, 12)
            for s in range(NT + 3):
                if s < NT:
                    i = s
                    if i >= 2:
                        pe.wait_ge(y3_used, i - 1)
                    for h in range(2):
                        for j in range(KD):
                            last = mm(ps[:, 2 * (i % 2) + h, :], yT[:, j, tile(i)], w_out[:, j, h * 512:(h + 1) * 512],
                                      start=(j == 0), stop=(j == KD - 1))
                    last.then_inc(w3_mm, 1)
                i = s - 2
                if 0 <= i < NT:
                    pe.wait_ge(h2_ready, i + 1)
                    if i:
                        pe.wait_ge(h2T_ready, i)
                    for j in range(KD):
                        last = pe.transpose(ps[:, 4 + j // 4, (j % 4) * P:(j % 4 + 1) * P], h2[:, i % 2, j * P:(j + 1) * P],
                                            ident)
                    last.then_inc(h2_t, 1)
                i = s - 3
                if 0 <= i < NT:
                    if i == 0:
                        pe.wait_ge(router_in, 32)
                    pe.wait_ge(h2T_ready, i + 1)
                    for j in range(KD):
                        last = mm(ps[:, 6 + i // ST, (i % ST) * E:(i % ST + 1) * E], h2T[:, i % 2, j, :], w_router[:, j, :],
                                  start=(j == 0), stop=(j == KD - 1))
                    last.then_inc(router_mm, 1)
            pe.wait_ge(h2T_ready, NT)
            for k in range(4):
                if k >= 2:
                    pe.wait_ge(g2_ready, k - 1)
                rows(lambda m: modT[:, 40 + 4 * (k % 2) + m, k // 2:k // 2 + 1], k, 4 + k % 2, g2_mm)
            pe.wait_ge(sel_ready, 1)
            pe.wait_ge(y3_used, NT)
            for i in range(NT):
                dst = ps[:, i // ST, (i % ST) * E:(i % ST + 1) * E]
                mm(dst, tri_b, sel_b[:, i, :], start=True, stop=(i == 0))
                for t in range(i):
                    mm(dst, ones_b, sel_b[:, t, :], start=False, stop=(t == i - 1))
            for i in range(NT):
                last = mm(ps[0:E, 2, 0:1], sel_b[:, i, :], ones_b[:, 0:1], start=(i == 0), stop=(i == NT - 1))
            last.then_inc(rank_mm, 1)
            pe.wait_ge(nb_ready, 1)
            mm(ps[0:E, 3, 0:1], C["tri64i"][0:E], cnt_f, start=True, stop=True)
            mm(ps[0:1, 3, 64:64 + E], cnt_f, C["tri64i"][0:E], start=True, stop=True).then_inc(end_mm, 1)
            pe.wait_ge(cmp_ready, 1)
            mm(ps[:, 6, 0:NBP], nb_bc, cmp_b, start=True, stop=True)
            mm(ps[0:1, 7, 0:NBP], ones[0:E, :], cmp_b, start=True, stop=True).then_inc(blk_mm, 1)
            pe.wait_ge(tables_ready, 1)
            pe.wait_ge(g2_ready, 4)
            w4 = wexp.rearrange("p s (t j n) -> p s t j n", t=3, j=KD)
            wd = wexp[:, :, 4096:EW].rearrange("p s (j n) -> p s j n", j=2)

            def step(n, p):
                dyn = not isinstance(n, int)
                p %= 2
                if dyn:
                    pe.wait_ge(h_ready, n + 1)
                    pe.wait_ge(tables_ready, 1)
                    for j in range(2):
                        last = pe.transpose(ps[:, 6, j * P:(j + 1) * P], h_sb[:, p, j * P:(j + 1) * P], ident)
                    last.then_inc(ht_mm, 1)
                if dyn or n + 2 >= 0:
                    pe.wait_ge(xg_in[p], 16 * ((n - p) // 2 + 2) if not dyn else (n - p) * 8 + 32)
                    at_least(pe, xT_ready, n + 2)
                    pe.wait_ge(tables_ready, 1)
                    for j in range(KD):
                        last = pe.transpose(ps[:, j // 4, (j % 4) * P:(j % 4 + 1) * P], xg[:, p, j * P:(j + 1) * P], ident)
                    last.then_inc(x_t, 1)
                if dyn or n + 1 >= 0:
                    e = expert_of(pe, n + 1)
                    slot = pe.snap(e % SLOTS)
                    pe.wait_ge(xT_ready, n + 2)
                    pe.wait_ge(experts_ready, e + 1)
                    pe.wait_ge(tables_ready, 1)
                    for j in range(KD):
                        last = mm(ps[:, 3 - p, :].rearrange("p (t n) -> p t n", t=2), xT[:, 1 - p, j, :],
                                  w4[:, bass.ds(slot, 1), 0:2, j, :].rearrange("p s t n -> p (s t) n"),
                                  start=(j == 0), stop=(j == KD - 1))
                    last.then_inc(gu_mm, 1)
                if dyn or n + 4 >= 0:
                    pe.wait_ge(hot_ready, n + 5)
                    at_least(pe, idx_ready, n + 4)
                    pe.wait_ge(tables_ready, 1)
                    for i in range(NT):
                        last = mm(ps[:, 7, 0:3], hot[:, p, i, :], idcol_b[:, i, :], start=(i == 0), stop=(i == NT - 1))
                    last.then_inc(list_mm, 1)
                if dyn:
                    e = expert_of(pe, n)
                    slot = pe.snap(e % SLOTS)
                    pe.wait_ge(hT_ready, n + 1)
                    pe.wait_ge(y_ready, n + PRIME)
                    pe.wait_ge(tables_ready, 1)
                    for h in range(2):
                        for j in range(2):
                            last = mm(ps[:, 4 + h, :], hTe[:, p, j, :],
                                      wd[:, bass.ds(slot, 1), j, h * 512:(h + 1) * 512].rearrange("p s n -> p (s n)"),
                                      start=(j == 0), stop=(j == 1))
                    last.then_inc(y_mm, 1)

            block_steps(pe, step)

        def phase3_dve(dve, done, variance, normalise):
            tt, ts, stt = dve.tensor_tensor, dve.tensor_scalar, dve.scalar_tensor_tensor
            two = lambda x: x.rearrange("p (h x) -> p h x", h=2)
            dve.wait_ge(row_ready, 12)
            dve.wait_ge(s_zero, 2)
            k = 2 * NT + 1
            for s in range(NT + 1):
                i = s
                if i < NT:
                    c = cond_of(i)
                    x = x1[:, i % 2, :]
                    dve.wait_ge(w3_mm, i + 1)
                    if i >= 2:
                        dve.wait_ge(x1_out[i % 2], 16 * (i // 2))
                    tt(two(x), ps[:, 2 * (i % 2):2 * (i % 2) + 2, :], two(g1_row[:, c, :]), ALU.mult).then_inc(y3_used, 1)
                    dve.wait_ge(y3_used, i + 1)
                    dve.wait_ge(x0r_in[i % 2], 16 * (i // 2 + 1))
                    done(stt(x, x0[:, i % 2, :], ALPHA, x, ALU.mult, ALU.add))
                    variance(k, (x[:, 0:512], x[:, 512:D]))
                    normalise(k, x, x).then_inc(xa_raw, 1)
                    k += 1
                i = s - 1
                if i >= 0:
                    c = cond_of(i)
                    x = x1[:, i % 2, :]
                    dve.wait_ge(x1_ready, i + 1)
                    variance(k, (x[:, 0:512], x[:, 512:D]))
                    y = h2n[:, i % 2, :]
                    done(normalise(k, y, x))
                    k += 1
                    done(tt(y, y, sc2_row[:, c, :], ALU.mult))
                    if i >= 2:
                        dve.wait_ge(h2_out[i % 2], 16 * (i // 2))
                        dve.wait_ge(h2_t, i - 1)
                    tt(h2[:, i % 2, :].rearrange("p (j q) -> p q j", j=KD), y.rearrange("p (q j) -> p q j", j=KD),
                       sh2_row[:, c, :].rearrange("p (q j) -> p q j", j=KD), ALU.add).then_inc(h2_ready, 1)
            flat = lambda v: v.rearrange("p i e -> p (i e)")
            grp = lambda v: flat(v).rearrange("p (g m) -> p g m", m=NGRP)
            dve.tensor_copy(tri_b, C["tri"])
            dve.memset(ones_b, 1.0)
            done(dve.memset(wrow, 0.0))
            done(dve.memset(wrow[:, :, 0:1], 1.0))
            dve.wait_ge(score_ready, 1)
            dve.wait_ge(router_in, 32)
            done(tt(biased, scores, rbias.unsqueeze(1).to_broadcast((P, NT, E)), ALU.add))
            done(dve.tensor_reduce(gm1, grp(biased), AX, ALU.max))
            bc = lambda v: v.unsqueeze(2).to_broadcast((P, NT * NGRP, NGRP))
            done(tt(grp(rbuf), grp(biased), bc(gm1), ALU.is_equal))
            dve.tensor_reduce(gcnt, grp(rbuf), AX, ALU.add)
            done(stt(flat(rbuf2), flat(rbuf), -BIG, flat(biased), ALU.mult, ALU.add))
            dve.tensor_reduce(gm2, grp(rbuf2), AX, ALU.max)
            done(ts(gcnt, gcnt, 2.0, 1.0, ALU.is_ge, ALU.subtract))
            done(stt(gtmp, gcnt, BIG, gm1, ALU.mult, ALU.add))
            done(tt(gm2, gm2, gtmp, ALU.max))
            done(tt(gsum, gm1, gm2, ALU.add))
            g3 = gsum.rearrange("p (i g) -> p i g", g=NGRP)
            other = g3.unsqueeze(2).to_broadcast((P, NT, NGRP, NGRP))
            own = g3.unsqueeze(3).to_broadcast((P, NT, NGRP, NGRP))
            v4 = lambda v: v.rearrange("p i (g m) -> p i g m", m=NGRP)
            tt(v4(rbuf), other, own, ALU.is_gt)
            done(tt(v4(rbuf2), other, own, ALU.is_equal))
            done(tt(rbuf2, rbuf2, C["low8"].unsqueeze(1).to_broadcast((P, NT, E)), ALU.mult))
            done(tt(rbuf, rbuf, rbuf2, ALU.add))
            done(dve.tensor_reduce(gcnt, grp(rbuf), AX, ALU.add))
            done(ts(gcnt, gcnt, float(TOPG), 1.0, ALU.is_lt, ALU.subtract))
            done(stt(grp(rbuf), bc(gcnt), BIG, grp(biased), ALU.mult, ALU.add))
            done(dve.max(top8[:, 0, :], rbuf[:, 0, :]))
            for i in range(NT):
                if i + 1 < NT:
                    dve.max(top8[:, (i + 1) % 2, :], rbuf[:, i + 1, :])
                done(dve.match_replace(rbuf2[:, i, :], top8[:, i % 2, :], rbuf[:, i, :], -3 * BIG))
            done(ts(flat(sel), flat(rbuf2), -2 * BIG, None, ALU.is_le))
            dve.tensor_copy(flat(sel_b), flat(sel)).then_inc(sel_ready, 1)
            done(tt(rbuf, scores, sel, ALU.mult))
            done(dve.tensor_reduce(den, rbuf, AX, ALU.add))
            done(dve.reciprocal(den, den))
            done(ts(den, den, SCALE, None, ALU.mult))
            tt(wrow[:, :, 1:NE], rbuf, den.unsqueeze(2).to_broadcast((P, NT, E)), ALU.mult).then_inc(wrow_ready, 1)
            dve.wait_ge(rank_mm, 1)
            done(ts(cnt_i, ps[0:E, 2, 0:1], float(P - 1), None, ALU.add))
            done(ts(cnt_i, cnt_i, 7, None, ALU.logical_shift_right))
            done(dve.tensor_copy(cnt_f, cnt_i))
            done(ts(cnt_f, cnt_f, 1.0, None, ALU.max))
            ts(nb_bc, cnt_f.to_broadcast((E, P)), C["pastend"][0:E], None, ALU.add).then_inc(nb_ready, 1)
            dve.wait_ge(router_mm, NT)
            dve.wait_ge(x1_out[0], 16 * 5)
            dve.wait_ge(x1_out[1], 16 * 4)
            dve.tensor_copy(keytab[:, :, 0], C["tokid"])
            stt(keytab[:, 0:ST, 1:NE], ps[:, 0, :].rearrange("p (i e) -> p i e", e=E), 1.0, sel[:, 0:ST, :], ALU.add, ALU.mult)
            done(stt(keytab[:, ST, 1:NE], ps[:, 1, 0:E], 1.0, sel[:, ST, :], ALU.add, ALU.mult))
            ts(keytab[:, :, 1:NE], keytab[:, :, 1:NE], -1.0, None, ALU.add)
            dve.tensor_copy(flat(idcol_b), C["idcol"])
            dve.wait_ge(end_mm, 1)
            dve.tensor_copy(endc, ps[0:E, 3, 0:1])
            dve.memset(endtab[0:1, 0:1], NT)
            done(ts(endtab[0:1, 1:NE], ps[0:1, 3, 64:64 + E], float(NT), None, ALU.add))
            ts(cmp_b, C["blk"][0:E], endc, None, ALU.is_ge).then_inc(cmp_ready, 1)
            dve.wait_ge(blk_mm, 1)
            stt(r0tab, ps[:, 6, 0:NBP], -float(P), C["r0"], ALU.mult, ALU.add)
            done(tt(etmp, ps[0:1, 7, 0:NBP], C["isroute"][0:1], ALU.add))
            ts(etab, etmp, float(E), None, ALU.min).then_inc(tables_ready, 1)
            dve.wait_ge(tables_ready, 1)

            def chain(ins, n, m, k):
                ins.then_inc(blk_step, 1)
                dve.wait_ge(blk_step, m * (n + LOOK + 1) + k + 1)

            def step(n, p):
                dyn = not isinstance(n, int)
                p %= 2
                if dyn or n + 2 >= 0:
                    e = expert_of(dve, n + 2)
                    dve.wait_ge(xg_in[p], 16 * ((n - p) // 2 + 2) if not dyn else (n - p) * 8 + 32)
                    if dyn:
                        dve.wait_ge(y_ready, n + 1)
                    w = dve.snap((n + 2) % 4)
                    dve.wait_ge(tables_ready, 1)
                    dve.tensor_copy(wcol[:, bass.ds(w, 1)], xg[:, p, bass.ds(e + D, 1)]).then_inc(wcol_ready, 1)
                if dyn:
                    dve.wait_ge(sums_done, n + 1)
                    dve.wait_ge(tables_ready, 1)
                    dve.tensor_copy(sidx[:, p:p + 1], idxtab[:, bass.ds(n, 1)]).then_inc(sidx_ready, 1)
                if dyn or n + 1 >= 0:
                    dve.wait_ge(sg_ready, n + 2)
                    dve.wait_ge(tables_ready, 1)
                    tt(h_sb[:, 1 - p, :].rearrange("p (j q) -> p q j", j=2),
                       ps[:, 3 - p, FF:2 * FF].rearrange("p (q j) -> p q j", j=2),
                       sg[:, 1 - p, :].rearrange("p (q j) -> p q j", j=2), ALU.mult).then_inc(h_ready, 1)
                if dyn or n + 4 >= 0:
                    dve.wait_ge(list_mm, n + 5)
                    dve.wait_ge(tables_ready, 1)
                    chain(dve.tensor_copy(lst[:, 0:3], ps[:, 7, 0:3]), n, 5, 0)
                    chain(stt(lst[:, 0:1], lst[:, 2:3], C["negslot"], lst[:, 0:1], ALU.mult, ALU.add), n, 5, 1)
                    ts(gidx[:, p:p + 1], lst[:, 0:1], C["trash"], lst[:, 1:2], ALU.add, ALU.add).then_inc(idx_ready, 1)
                    dve.wait_ge(idx_ready, n + 5)
                    chain(dve.tensor_copy(idxtab[:, bass.ds(n + 4, 1)], gidx[:, p:p + 1]), n, 5, 2)
                else:
                    for k in range(3):
                        dve.nop().then_inc(blk_step, 1)
                b = n + 5
                e = expert_of(dve, b)
                dve.wait_ge(tables_ready, 1)
                chain(ts(rc[:, 1 - p, 0:NT], keytab[:, :, bass.ds(e, 1)].rearrange("p i o -> p (i o)"),
                         r0tab[:, bass.ds(b, 1)], None, ALU.subtract), n, 5, 3)
                at_least(dve, list_mm, n + 4)
                dve.wait_ge(tables_ready, 1)
                tt(hot[:, 1 - p], C["slot"].unsqueeze(1).to_broadcast((P, NT, P)),
                   rc[:, 1 - p, 0:NT].unsqueeze(2).to_broadcast((P, NT, P)), ALU.is_equal).then_inc(hot_ready, 1)
                dve.wait_ge(hot_ready, n + 6)
                dve.nop().then_inc(blk_step, 1)

            block_steps(dve, step)
            dve.wait_ge(ln2_in, 32)
            for i in range(NT):
                c = cond_of(i)
                dve.wait_ge(fin_in[i % FR], 32 * (i // FR + 1))
                x, y = acc_t[:, i % FR, :], x1_t[:, i % FR, :]
                done(tt(x, x, g2_row[:, c, :], ALU.mult))
                done(stt(x, y, ALPHA, x, ALU.mult, ALU.add))
                variance(k, (x[:, 0:512], x[:, 512:D]))
                normalise(k, x, x).then_inc(fin_raw, 1)
                k += 1

        @block.sync
        def _(sp):
            sp.dma_start(cond_rows[0:8, :], A["c"].rearrange("a (j p) -> (a j) p", p=P)).then_inc(cond_in, 16)
            sp.dma_start(cond_rows[8:16, :], A["c_ctx"].rearrange("(j p) -> j p", p=P)).then_inc(cond_in, 16)
            sp.dma_start(bada_rows, A["b_ada"].rearrange("a (m p) -> (a m) p", p=P)).then_inc(cond_in, 16)
            for n, (src, c0, w) in enumerate(STREAM):
                if n >= RING:
                    sp.wait_ge(w_used, n - RING + 1)
                sp.dma_start(ring[:, n % RING, :, 0:w], src[:, :, c0:c0 + w]).then_inc(w_in[n % RING], 16)
            sp.wait_ge(sgu_done, NT)
            sp.wait_ge(conv_done, 2)
            sp.dma_start(w_out, A["w_out"][0].rearrange("(j p) n -> p j n", p=P)).then_inc(wout_in, 16)
            phase3_sync(sp)

        @block.gpsimd
        def _(pool):
            pool.dma_start(const[:, :], A["constants"]).then_inc(const_in, 16)
            for h in range(2):
                pool.dma_start(pcol[h * GRID:(h + 1) * GRID, :], A["pos_col"]).then_inc(const_in, 16)

            def load_x(i):
                if i < ST:
                    pool.dma_start(xin[:, i % 2, :], A["x_sample"][0, tile(i), :]).then_inc(x_in[i % 2], 16)
                    pool.dma_start(prow[:, i % 2, :], A["pos_row"][2 * i:2 * i + 2, :].unsqueeze(1)
                                   .to_broadcast((2, GRID, 512))).then_inc(x_in[i % 2], 16)
                else:
                    pool.dma_start(xin[:, i % 2, :], A["x_prompt"][0]).then_inc(x_in[i % 2], 16)

            load_x(0)
            load_x(1)
            step = [0]

            def done(ins):
                step[0] += 1
                ins.then_inc(pool_step, 1)
                pool.wait_ge(pool_step, step[0])

            done(pool.memset(wgla[0:32, :], 0.0))
            done(pool.memset(lrT[32:33, :], 1.0))
            done(pool.memset(ones, 1.0))
            for d in range(2):
                pool.dma_start(wgla[d * LR:(d + 1) * LR, d * W:(d + 1) * W], A["w_gla_a"][0, d]).then_inc(gate_in, 16)
            pool.dma_start(wgla[32:33, :], A["b_gla_a"].rearrange("a d w -> a (d w)")).then_inc(gate_in, 16)
            pool.dma_start(gng, A["gla_norm_g"].rearrange("a (j p) -> p (a j)", p=P),
                           allow_slow_non_contiguous=True).then_inc(gate_in, 16)
            pool.dma_start(wcv, A["w_conv"][0].rearrange("w (j p) -> p w j", p=P),
                           allow_slow_non_contiguous=True).then_inc(gate_in, 16)
            pool.dma_start(sgu_gb[:, 0, :], A["sgu_norm_g"][0].partition_broadcast(P)).then_inc(sgu_in, 16)
            pool.dma_start(sgu_gb[:, 1, :], A["sgu_norm_b"][0].partition_broadcast(P)).then_inc(sgu_in, 16)
            for j in range(2):
                for h in range(2):
                    pool.dma_start(bsgu[h * 64:(h + 1) * 64, j, :],
                                   A["b_sgu"][0, 2 * j + h].partition_broadcast(64)).then_inc(sgu_in, 16)
            for i in range(NT):
                pool.wait_ge(x0_ready, i + 1)
                pool.dma_start(x0_dram[tile(i), :], xin[:, i % 2, :]).then_inc(x0_out[i % 2], 16)
                if i + 2 < NT:
                    pool.wait_ge(x0_out[i % 2], 16 * (i // 2 + 1))
                    pool.wait_ge(xn_ready, i + 1)
                    load_x(i + 2)
            pool.wait_ge(x0_out[0], 16 * 5)
            pool.wait_ge(x0_out[1], 16 * 4)
            pool.wait_ge(xn_ready, NT)
            for z in (zc, zx):
                for a, b in ((0, 1), (SAMPLE + 1, SAMPLE + 3), (T + 3, T + 4)):
                    last = pool.memset(z[:, :, a:b], 0.0)
            last.then_inc(pads, 1)
            pool.wait_ge(pads, 1)
            pool.dma_start(wsgu, A["w_sgu"][0].rearrange("g s t -> s g t")).then_inc(sgu_in, 16)
            pool.wait_ge(w_used, ADA1 + len(PROJ))
            pool.dma_start(dft_f, A["dft_feat"].rearrange("p (k n) -> p k n", k=3)).then_inc(dft_in, 16)
            pool.dma_start(dft_t, A["dft_tok"].rearrange("p (f d n) -> p f d n", f=2, d=9)).then_inc(dft_in, 16)
            pool.wait_ge(evac, ev_after["ft"])
            f8 = ftT[:, :, 0:SAMPLE].rearrange("p j (a b) -> p j a b", a=8)
            tt = pool.tensor_tensor
            tt(bs, f8[:, :, 0:4, :], f8[:, :, 4:8, :], ALU.add)
            done(tt(bm, f8[:, :, 0:4, :], f8[:, :, 4:8, :], ALU.subtract))
            tt(bpq, bs[:, :, 0:2, :], bs[:, :, 2:4, :], ALU.add)
            tt(fr[:, 2], bs[:, :, 0, :], bs[:, :, 2, :], ALU.subtract)
            tt(fr[:, 3], bs[:, :, 1, :], bs[:, :, 3, :], ALU.subtract)
            tt(buv[:, :, 0, :], bm[:, :, 1, :], bm[:, :, 3, :], ALU.subtract)
            done(tt(buv[:, :, 1, :], bm[:, :, 1, :], bm[:, :, 3, :], ALU.add))
            tt(fr[:, 0], bpq[:, :, 0, :], bpq[:, :, 1, :], ALU.add)
            tt(fr[:, 1], bpq[:, :, 0, :], bpq[:, :, 1, :], ALU.subtract)
            done(pool.tensor_scalar(buv, buv, float(np.sqrt(0.5)), None, ALU.mult))
            tt(fr[:, 4], bm[:, :, 0, :], buv[:, :, 0, :], ALU.add)
            tt(fr[:, 6], bm[:, :, 0, :], buv[:, :, 0, :], ALU.subtract)
            tt(fr[:, 5], bm[:, :, 2, :], buv[:, :, 1, :], ALU.add)
            tt(fr[:, 7], bm[:, :, 2, :], buv[:, :, 1, :], ALU.subtract).then_inc(fr_ready, 1)
            for i in range(NT):
                pool.wait_ge(vn_raw, i + 1)
                if i == 0:
                    pool.wait_ge(sgu_in, 16 * 7)
                done(tt(vn[:, i % 2, :], vn[:, i % 2, :], sgu_gb[:, 0, :], ALU.mult))
                tt(vn[:, i % 2, :], vn[:, i % 2, :], sgu_gb[:, 1, :], ALU.add).then_inc(vn_ready, 1)
            pool.wait_ge(w_used, len(STREAM))
            pool.memset(S, 0.0).then_inc(s_zero, 1)
            pool.wait_ge(s_zero, 1)
            for d in range(2):
                for h in range(2):
                    pool.dma_start(S[h * 64:(h + 1) * 64, 0, 2 * d:2 * d + 2, h * 64:(h + 1) * 64],
                                   A["state_gla"][0, 0, d].rearrange("(q h) k v -> h k q v", h=2)[h]).then_inc(s_init, 16)
            pool.wait_ge(S_ready, 2 * NT)
            for d in range(2):
                for h in range(2):
                    pool.dma_start(out_state[0, 0, d].rearrange("(q h) k v -> h k q v", h=2)[h],
                                   S[h * 64:(h + 1) * 64, (2 * ST + 2) % 4, 2 * d:2 * d + 2, h * 64:(h + 1) * 64]
                                   ).then_inc(state_out, 16)
            pool.wait_ge(state_out, 64)
            phase3_pool(pool, done)

        @block.scalar
        def _(act):
            a = act.activation
            act.wait_ge(cond_t, 1)
            a(cs, ps[:, 0, 0:16].rearrange("p (c j) -> p c j", c=2), ACT.Silu).then_inc(cs_ready, 1)
            r = 0

            def inv_std(k):
                act.wait_ge(ivar_ready, k + 1)
                a(rstd[:, k % 2:k % 2 + 1], ivar[:, k % 2:k % 2 + 1], ACT.Sqrt).then_inc(rstd_ready, 1)

            for i in range(ST):
                inv_std(i)
            act.wait_ge(mod_ready, 1)
            for g, (i0, i1) in enumerate(GROUPS):
                c = g // 2
                if g == 1:
                    inv_std(ST)
                for j in range(KD):
                    r += 1
                    act.wait_ge(ring_mm, r)
                    a(hT[:, j, i0 * P:i1 * P], ps[:, 2 + (r - 1) % 4, 0:(i1 - i0) * P], ACT.Identity,
                      scale=scp[:, j, c:c + 1], bias=modT[:, j, c:c + 1]).then_inc(evac, 1)
            for n in PROJ:
                if n == "cvc":
                    act.wait_ge(x0_out[0], 16 * 5)
                    act.wait_ge(x0_out[1], 16 * 4)
                for j in range(max(1, COL[n][1] // P)):
                    for i0, i1 in GROUPS:
                        r += 1
                        act.wait_ge(ring_mm, r)
                        src = ps[:, 2 + (r - 1) % 4, 0:(i1 - i0) * P]
                        cols = slice(i0 * P, i1 * P)
                        if n in ("cvc", "cvx"):
                            off = 1 if i0 < ST else 3
                            dst = (zc if n == "cvc" else zx)[:, j, i0 * P + off:i1 * P + off]
                            a(dst, src, ACT.Copy).then_inc(evac, 1)
                        elif n == "lr":
                            a(lrT[0:32, cols], src[0:32], ACT.Copy).then_inc(evac, 1)
                        elif n == "go":
                            a(DEST[n][:, j, cols], src, ACT.Silu).then_inc(evac, 1)
                        elif n == "q":
                            a(DEST[n][:, j, cols], src, ACT.Copy, scale=DK ** -0.5).then_inc(evac, 1)
                        else:
                            a(DEST[n][:, j, cols], src, ACT.Copy).then_inc(evac, 1)
            for i in range(NT):
                inv_std(NT + i)
            for d in range(9):
                act.wait_ge(uv_mm, d + 1)
                if d >= 2:
                    act.wait_ge(ft_mm, d - 1)
                a(uv[:, d % 2, :], ps[:, d % 2, :], ACT.Copy).then_inc(uv_ready, 1)
            for s in range(NT + 4):
                if s < NT:
                    u = s
                    act.wait_ge(logit_mm, u + 1)
                    if u:
                        act.wait_ge(la_ready, u)
                    a(na, ps[:, 0, :], ACT.Abs).then_inc(act_step, 1)
                    act.wait_ge(act_step, 2 * u + 1)
                    a(na, na, ACT.Exp, scale=-1.0).then_inc(act_step, 1)
                    act.wait_ge(act_step, 2 * u + 2)
                    a(na, na, ACT.Ln, bias=1.0).then_inc(ln_ready, 1)
                u = s - 1
                if 0 <= u < NT:
                    act.wait_ge(bg_mm, u + 1)
                    if u >= 2:
                        act.wait_ge(S_ready, 2 * (u - 1))
                        act.wait_ge(kv_mm, u - 1)
                    a(e1[:, u % 2].rearrange("p a b -> p (a b)"), ps[:, 1, :], ACT.Exp).then_inc(e_ready, 1)
                    a(ki[:, u % 2].rearrange("p a b -> p (a b)"), ps[:, 1, :], ACT.Exp, scale=-1.0).then_inc(e_ready, 1)
                    a(ke[:, u % 2], ps[:, 2, :], ACT.Exp).then_inc(e_ready, 1)
                    act.wait_ge(kv_t, u + 1)
                    if u >= 3:
                        act.wait_ge(o_mm, u - 2)
                    for d in range(2):
                        a(vt[:, u % 3, d * W:(d + 1) * W], ps[:, 4, d * W:(d + 1) * W], ACT.Copy).then_inc(v_ready, 1)
            act.wait_ge(ivar_ready, 2 * NT + 1)
            a(rms, rms, ACT.Sqrt).then_inc(rstd_ready, 1)
            phase3_act(act, inv_std)

        @block.vector
        def _(dve):
            step = [0]

            def done(ins):
                step[0] += 1
                ins.then_inc(dve_step, 1)
                dve.wait_ge(dve_step, step[0])

            dve.wait_ge(cond_t, 1)
            dve.tensor_copy(badaT, ps[:, 6, 0:48]).then_inc(bada_ready, 1)
            dve.wait_ge(const_in, 48)

            def variance(k, src_halves):
                for h, src in enumerate(src_halves):
                    last = dve.bn_stats(st6[:, h, :], src)
                done(last)
                done(dve.bn_aggr(mv[:, k % 2], st6[:, 0:len(src_halves)].rearrange("p a s -> p (a s)")))
                done(dve.tensor_scalar(ivar[:, k % 2:k % 2 + 1], mv[:, k % 2, 1:2], LN_EPS, None, ALU.add))
                dve.reciprocal(ivar[:, k % 2:k % 2 + 1], ivar[:, k % 2:k % 2 + 1]).then_inc(ivar_ready, 1)

            def normalise(k, out, x):
                dve.wait_ge(rstd_ready, k + 1)
                return dve.tensor_scalar(out, x, mv[:, k % 2, 0:1], rstd[:, k % 2:k % 2 + 1], ALU.subtract, ALU.mult)

            def add_position(i):
                dve.wait_ge(x_in[i % 2], 32 * (i // 2 + 1) if i < ST else 32 * (ST // 2) + 16)
                x = xin[:, i % 2, :]
                if i < ST:
                    dve.tensor_tensor(x[:, 0:512], x[:, 0:512], prow[:, i % 2, :], ALU.add)
                    dve.tensor_tensor(x[:, 512:D], x[:, 512:D], pcol, ALU.add).then_inc(x0_ready, 1)
                    dve.wait_ge(x0_ready, i + 1)
                else:
                    dve.nop().then_inc(x0_ready, 1)
                variance(i, (x[:, 0:512], x[:, 512:D]))

            add_position(0)
            for i in range(NT):
                if i + 1 < NT:
                    add_position(i + 1)
                g = min(i // 4, 2)
                if g == 2:
                    dve.wait_ge(ring_mm, KD)
                normalise(i, xn[:, g % 2, i - GROUPS[g][0], :], xin[:, i % 2, :]).then_inc(xn_ready, 1)
                if i == 3:
                    dve.wait_ge(ada_mm, 1)
                    dve.wait_ge(bada_ready, 1)
                    done(dve.tensor_tensor(modT[:, 0:16, :], ps[:, 1, 0:32].rearrange("p (m c) -> p m c", c=2),
                                           badaT[:, 0:16].unsqueeze(2).to_broadcast((P, 16, 2)), ALU.add))
                    dve.tensor_scalar(scp, modT[:, 8:16, :], 1.0, None, ALU.add).then_inc(mod_ready, 1)
            dve.wait_ge(evac, ev_after["cvb"])
            dve.wait_ge(pads, 1)
            dve.wait_ge(gate_in, 80)
            for j in range(2):
                done(dve.tensor_tensor(zx[:, j, :], zc[:, j, :], zx[:, j, :], ALU.mult))
                n = ZW - 2
                done(dve.tensor_scalar(zt[:, 1:1 + n], zx[:, j, 0:n], wcv[:, 0, j:j + 1], None, ALU.mult))
                done(dve.scalar_tensor_tensor(zt[:, 1:1 + n], zx[:, j, 1:1 + n], wcv[:, 1, j:j + 1], zt[:, 1:1 + n],
                                              ALU.mult, ALU.add))
                done(dve.scalar_tensor_tensor(zt[:, 1:1 + n], zx[:, j, 2:2 + n], wcv[:, 2, j:j + 1], zt[:, 1:1 + n],
                                              ALU.mult, ALU.add))
                dve.tensor_tensor(yT[:, 4 + j, 0:SAMPLE], yT[:, 4 + j, 0:SAMPLE], zt[:, 1:SAMPLE + 1], ALU.mult)
                dve.tensor_tensor(yT[:, 4 + j, SAMPLE:T], yT[:, 4 + j, SAMPLE:T], zt[:, SAMPLE + 3:T + 3], ALU.mult)\
                   .then_inc(conv_done, 1)
            dve.wait_ge(ada_mm, 2)
            done(dve.tensor_tensor(modT[:, 16:48, :], ps[:, 7, 0:64].rearrange("p (m c) -> p m c", c=2),
                                   badaT[:, 16:48].unsqueeze(2).to_broadcast((P, 32, 2)), ALU.add))
            dve.tensor_scalar(scp2, modT[:, 32:40, :], 1.0, None, ALU.add).then_inc(mod_ready, 1)
            dve.wait_ge(sgu_wt, 1)
            dve.tensor_copy(wsguT[:, :, :], ps[:, 0, :].rearrange("p (g s) -> p g s", g=4)).then_inc(sgu_wt_ready, 1)

            def sgu_norm(i):
                dve.wait_ge(sgv_t, i + 1)
                src = ps[:, 2 + i % 2, 0:W]
                variance(NT + i, (src,))
                if i >= 2:
                    dve.wait_ge(sp_mm, i - 1)
                normalise(NT + i, vn[:, i % 2, :], src).then_inc(vn_raw, 1)

            def sgu_mult(i):
                dve.wait_ge(sp_mm, i + 1)
                src = ps[:, 4 + i % 2, 0:2 * P].rearrange("p (j s) -> p j s", j=2)
                if i == 0:
                    dve.wait_ge(sgu_in, 16 * 7)
                done(dve.tensor_tensor(src, src, bsgu[:, :, :], ALU.add))
                y = yT[:, 2:4, tile(i)]
                dve.tensor_tensor(y, src, y, ALU.mult).then_inc(sgu_done, 1)

            sgu_norm(0)
            for i in range(NT):
                if i + 1 < NT:
                    sgu_norm(i + 1)
                sgu_mult(i)
            dve.wait_ge(ft_mm, 9)
            for j in range(2):
                for h in range(2):
                    dve.tensor_copy(yT[:, 6 + j, 0:SAMPLE].rearrange("p (c d) -> p d c", d=8)[:, 4 * h:4 * h + 4, :],
                                    ps[:, 2 + 2 * j + h, :].rearrange("p (d c) -> p d c", d=4))
            dve.tensor_copy(yT[:, 6:8, SAMPLE:T], ps[:, 6, 0:2 * P].rearrange("p (j c) -> p j c", j=2))\
               .then_inc(ft_done, 1)
            for s in range(NT + 3):
                u = s - 2
                if 0 <= u < NT:
                    dve.wait_ge(attn_mm, u + 1)
                    if u >= 2:
                        dve.wait_ge(o_mm, u - 1)
                    dve.tensor_tensor(am[:, u % 2, 0], ps[:, 5, :], C["mask"], ALU.mult)
                    dve.tensor_tensor(am[:, u % 2, 1], ps[:, 6, :], C["mask"], ALU.mult).then_inc(am_ready, 1)
                    dve.wait_ge(kv_mm, u + 1)
                    if u == 0:
                        dve.wait_ge(s_init, 64)
                    for half in range(2):
                        old = S[:, 4 if (u == ST and half == 0) else (2 * u + half) % 4]
                        new = S[:, (2 * u + half + 1) % 4]
                        if half or u:
                            dve.wait_ge(S_ready, 2 * u + half)
                        if half and u:
                            dve.wait_ge(o_mm, u)
                        for d in range(2):
                            c = half if d == 0 else 1 - half
                            edge = 64 * c + (63 if d == 0 else 0)
                            for q in range(2):
                                for h in range(2):
                                    hs = slice(h * 64, (h + 1) * 64)
                                    x = 2 * d + q
                                    last = dve.scalar_tensor_tensor(
                                        new[hs, x, hs], old[hs, x, hs], e1[hs, u % 2, x, edge:edge + 1],
                                        ps[hs, 3 + c, x * P + h * 64:x * P + (h + 1) * 64], ALU.mult, ALU.add)
                        last.then_inc(S_ready, 1)
                u = s - 3
                if 0 <= u < NT:
                    dve.wait_ge(o_mm, u + 1)
                    for d in range(2):
                        dst = o_tm[:, ft_tile(u, d), :]
                        src = ps[:, 7, d * W:(d + 1) * W]
                        if u < ST // 2 or (u == ST and d == 0):
                            last = dve.tensor_copy(dst, src)
                        else:
                            if u == ST:
                                last.then_inc(dve_step, 1)
                                step[0] += 1
                                dve.wait_ge(dve_step, step[0])
                            elif d == 0:
                                dve.wait_ge(o_acc, u)
                            last = dve.tensor_tensor(dst, src, dst, ALU.add)
                    last.then_inc(o_acc, 1)
                if s < NT:
                    u = s
                    dve.wait_ge(ln_ready, u + 1)
                    if u >= 2:
                        dve.wait_ge(bg_mm, u - 1)
                    dve.scalar_tensor_tensor(la[:, u % 2], ps[:, 0, :], 0.0, na, ALU.min, ALU.subtract)\
                       .then_inc(la_ready, 1)
                u = s - 1
                if 0 <= u < NT:
                    dve.wait_ge(e_ready, 3 * (u + 1))
                    dve.wait_ge(kv_t, u + 1)
                    if u >= 3:
                        dve.wait_ge(o_mm, u - 2)
                    for d in range(2):
                        cols = tile(ft_tile(u, d))
                        pr = slice(2 * d, 2 * d + 2)
                        dve.tensor_tensor(qd[:, u % 3, pr], qT[:, :, cols], e1[:, u % 2, pr], ALU.mult)
                        dve.tensor_tensor(ki[:, u % 2, pr], kT[:, :, cols], ki[:, u % 2, pr], ALU.mult)
                        last = dve.tensor_tensor(ke[:, u % 2, d * W:(d + 1) * W], ps[:, 3, d * W:(d + 1) * W],
                                                 ke[:, u % 2, d * W:(d + 1) * W], ALU.mult)
                    last.then_inc(qk_ready, 1)
            dve.wait_ge(o_acc, NT)
            o = o_tm.rearrange("p i w -> p (i w)")
            done(dve.tensor_tensor(osq, o, o, ALU.mult))
            done(dve.tensor_reduce(rms, osq.rearrange("p (g v) -> p g v", v=64), AX, ALU.add))
            done(dve.tensor_scalar(rms, rms, 1.0 / 64, RMS_EPS, ALU.mult, ALU.add))
            dve.reciprocal(rms, rms).then_inc(ivar_ready, 1)
            dve.wait_ge(rstd_ready, 2 * NT + 1)
            dve.tensor_tensor(o.rearrange("p (g v) -> p g v", v=64), o.rearrange("p (g v) -> p g v", v=64),
                              rms.unsqueeze(2).to_broadcast((P, NT * HEADS, 64)), ALU.mult).then_inc(o_ready, 1)
            n = 0
            for j in range(2):
                for i0, i1 in GROUPS:
                    n += 1
                    dve.wait_ge(o_t, n)
                    y = yT[:, j, i0 * P:i1 * P]
                    dve.scalar_tensor_tensor(y, ps[:, n % 2, 0:(i1 - i0) * P], gng[:, j:j + 1], y, ALU.mult, ALU.mult)\
                       .then_inc(gla_done, 1)
            phase3_dve(dve, done, variance, normalise)

        @block.tensor
        def _(pe):
            mm = pe.matmul
            pe.wait_ge(const_in, 48)
            pe.wait_ge(cond_in, 48)
            pe.transpose(ps[:, 0, 0:16], cond_rows, ident[0:16, 0:16])
            pe.transpose(ps[:, 6, 0:48], bada_rows, ident[0:48, 0:48]).then_inc(cond_t, 1)
            pe.wait_ge(cs_ready, 1)

            def loaded(n):
                pe.wait_ge(w_in[n % RING], 16 * (n // RING + 1))

            def ada(n0, n1, bank):
                for n in range(n0, n1):
                    loaded(n)
                    for h in range(2):
                        m = 2 * (n - n0) + h
                        for j in range(KD):
                            last = mm(ps[:, bank, 2 * m:2 * m + 2], ring[:, n % RING, j, h * P:(h + 1) * P], cs[:, :, j],
                                      start=(j == 0), stop=(j == KD - 1))
                    if n == n1 - 1:
                        last.then_inc(ada_mm, 1)
                        pe.wait_ge(ada_mm, 1 if bank == 1 else 2)
                        pe.nop().then_inc(w_used, 1)
                    else:
                        last.then_inc(w_used, 1)

            ada(0, ADA1, 1)
            r = 0
            for g, (i0, i1) in enumerate(GROUPS):
                pe.wait_ge(xn_ready, i1)
                for j in range(KD):
                    if r >= 4:
                        pe.wait_ge(evac, r - 3)
                    for i in range(i0, i1):
                        last = pe.transpose(ps[:, 2 + r % 4, (i - i0) * P:(i - i0 + 1) * P],
                                            xn[:, g % 2, i - i0, j * P:(j + 1) * P], ident)
                    last.then_inc(ring_mm, 1)
                    r += 1
            for k, name in enumerate(PROJ):
                n = ADA1 + k
                loaded(n)
                w = COL[name][1]
                chunks = max(1, w // P)
                m = min(w, P)
                for c in range(chunks):
                    for g, (i0, i1) in enumerate(GROUPS):
                        if k == 0 and c == 0:
                            pe.wait_ge(evac, KD * (g + 1))
                        pe.wait_ge(evac, r - 3)
                        for j in range(KD):
                            last = mm(ps[0:m, 2 + r % 4, 0:(i1 - i0) * P], ring[:, n % RING, j, c * P:c * P + m],
                                      hT[:, j, i0 * P:i1 * P], start=(j == 0), stop=(j == KD - 1))
                        last.then_inc(ring_mm, 1)
                        r += 1
                pe.wait_ge(ring_mm, r)
                pe.nop().then_inc(w_used, 1)
            ada(ADA1 + len(PROJ), len(STREAM), 7)
            pe.wait_ge(sgu_in, 16 * 7)
            for g in range(4):
                last = pe.transpose(ps[:, 0, g * P:(g + 1) * P], wsgu[:, g, :], ident)
            last.then_inc(sgu_wt, 1)
            pe.wait_ge(evac, EV_ALL)

            def sgv_transpose(i):
                if i >= 2:
                    pe.wait_ge(vn_raw, i - 1)
                for j in range(2):
                    last = pe.transpose(ps[:, 2 + i % 2, j * P:(j + 1) * P], sgvT[:, j, tile(i)], ident)
                last.then_inc(sgv_t, 1)

            sgv_transpose(0)
            sgv_transpose(1)
            for i in range(NT):
                if i == 0:
                    pe.wait_ge(sgu_wt_ready, 1)
                if i >= 2:
                    pe.wait_ge(sgu_done, i - 1)
                pe.wait_ge(vn_ready, i + 1)
                for g in range(4):
                    j, h = g // 2, g % 2
                    last = mm(ps[h * 64:(h + 1) * 64, 4 + i % 2, j * P:(j + 1) * P], vn[:, i % 2, g * 64:(g + 1) * 64],
                              wsguT[:, g, :], start=True, stop=True, skip_group_check=True)
                last.then_inc(sp_mm, 1)
                if i + 2 < NT:
                    sgv_transpose(i + 2)
            pe.wait_ge(dft_in, 32)
            pe.wait_ge(fr_ready, 1)

            def feature(d):
                if d >= 2:
                    pe.wait_ge(uv_ready, d - 1)
                for j in range(2):
                    terms = dft_terms(d) if d < 8 else [(None, 0)]
                    for t, (kind, f) in enumerate(terms):
                        lhsT = ftT[:, j, SAMPLE:T] if kind is None else fr[:, kind, j, :]
                        last = mm(ps[:, d % 2, j * W:(j + 1) * W], lhsT, dft_f[:, f, :], start=(t == 0),
                                  stop=(t == len(terms) - 1))
                last.then_inc(uv_mm, 1)

            pe.wait_ge(sgu_wt_ready, 1)
            feature(0)
            feature(1)
            pe.wait_ge(sgu_done, NT)
            for d in range(9):
                pe.wait_ge(uv_ready, d + 1)
                for j in range(2):
                    if d < 8:
                        dst = ps[:, 2 + 2 * j + d // 4, (d % 4) * P:(d % 4 + 1) * P]
                    else:
                        dst = ps[:, 6, j * P:(j + 1) * P]
                    for t in range(2):
                        last = mm(dst, uv[:, d % 2, (2 * j + t) * P:(2 * j + t + 1) * P], dft_t[:, t, d, :],
                                  start=(t == 0), stop=(t == 1))
                last.then_inc(ft_mm, 1)
                if d + 2 < 9:
                    feature(d + 2)
            pe.wait_ge(pads, 1)
            pe.wait_ge(gate_in, 80)
            pe.wait_ge(ft_done, 1)
            pe.wait_ge(mod_ready, 2)
            for s in range(NT + 3):
                u = s - 2
                if 0 <= u < NT:
                    pe.wait_ge(qk_ready, u + 1)
                    if u:
                        pe.wait_ge(am_ready, u)
                    for h in range(2):
                        for x in range(4):
                            hs = slice(h * 64, (h + 1) * 64)
                            last = mm(ps[:, 5 + h, x * P:(x + 1) * P], ki[hs, u % 2, x, :], qd[hs, u % 3, x, :],
                                      start=True, stop=True)
                    last.then_inc(attn_mm, 1)
                    pe.wait_ge(v_ready, 2 * (u + 1))
                    for c in range(2):
                        for x in range(4):
                            d, q = x // 2, x % 2
                            rows = slice(c * 64, (c + 1) * 64)
                            last = mm(ps[:, 3 + c, x * P:(x + 1) * P], ke[rows, u % 2, x * P:(x + 1) * P],
                                      vt[rows, u % 3, x * P:(x + 1) * P], start=True, stop=True)
                    last.then_inc(kv_mm, 1)
                u = s - 3
                if 0 <= u < NT:
                    pe.wait_ge(am_ready, u + 1)
                    pe.wait_ge(S_ready, 2 * u + 1)
                    if u:
                        pe.wait_ge(o_acc, u)
                    first = {0: True, 1: True}
                    for x in range(4):
                        d = x // 2
                        for lh in range(2):
                            half = lh if d == 0 else 1 - lh
                            st = S[:, 4 if (u == ST and half == 0) else (2 * u + half) % 4, x, :]
                            mm(ps[lh * 64:(lh + 1) * 64, 7, x * P:(x + 1) * P], qd[:, u % 3, x, lh * 64:(lh + 1) * 64], st,
                               start=first[lh], stop=True, skip_group_check=True)
                            first[lh] = False
                    for x in range(4):
                        for h in range(2):
                            vs = slice(x * P + h * 64, x * P + (h + 1) * 64)
                            last = mm(ps[:, 7, vs], am[:, u % 2, h, x * P:(x + 1) * P], vt[:, u % 3, vs],
                                      start=False, stop=True, skip_group_check=True)
                    last.then_inc(o_mm, 1)
                if s < NT:
                    u = s
                    if u:
                        pe.wait_ge(la_ready, u)
                    for d in range(2):
                        last = mm(ps[:, 0, d * W:(d + 1) * W], lrT[0:33, tile(ft_tile(u, d))], wgla[:, d * W:(d + 1) * W],
                                  start=True, stop=True)
                    last.then_inc(logit_mm, 1)
                u = s - 1
                if 0 <= u < NT:
                    pe.wait_ge(la_ready, u + 1)
                    if u:
                        pe.wait_ge(e_ready, 3 * u)
                    for x in range(4):
                        mm(ps[:, 1, x * P:(x + 1) * P], la[:, u % 2, x * P:(x + 1) * P],
                           C["cum"][:, (x // 2) * P:(x // 2 + 1) * P], start=True, stop=True)
                    for d in range(2):
                        last = mm(ps[:, 2, d * W:(d + 1) * W], C["suf"][:, d * P:(d + 1) * P],
                                  la[:, u % 2, d * W:(d + 1) * W], start=True, stop=True)
                    last.then_inc(bg_mm, 1)
                    if u:
                        pe.wait_ge(S_ready, 2 * u)
                    for d in range(2):
                        cols = tile(ft_tile(u, d))
                        for j in range(2):
                            pe.transpose(ps[:, 3, d * W + j * P:d * W + (j + 1) * P], kT[:, j, cols], ident)
                            last = pe.transpose(ps[:, 4, d * W + j * P:d * W + (j + 1) * P], vT[:, j, cols], ident)
                    last.then_inc(kv_t, 1)
            pe.wait_ge(o_ready, 1)
            pe.wait_ge(o_acc, NT)
            n = 0
            for j in range(2):
                for i0, i1 in GROUPS:
                    n += 1
                    if n > 2:
                        pe.wait_ge(gla_done, n - 2)
                    for i in range(i0, i1):
                        last = pe.transpose(ps[:, n % 2, (i - i0) * P:(i - i0 + 1) * P], o_tm[:, i, j * P:(j + 1) * P], ident)
                    last.then_inc(o_t, 1)
            phase3_pe(pe)


IN_NAMES = ["x_prompt", "x_sample", "c", "state_gla", "c_ctx", "w_ada", "b_ada", "w_in", "w_gla_a", "b_gla_a", "gla_norm_g",
            "sgu_norm_g", "sgu_norm_b", "w_sgu", "b_sgu", "w_conv", "w_out", "ln1_g", "ln1_b", "ln2_g", "ln2_b", "w_router",
            "router_bias", "w_exp_gate", "w_exp_up", "w_exp_down", "w_sh_gate", "w_sh_up", "w_sh_down"]


def kernel(**inputs):
    import concourse.bacc as bacc
    from concourse.bass_utils import run_bass_kernel_spmd

    nc = bacc.Bacc("TRN2", target_bir_lowering=False, num_devices=1)
    arrays = {n: np.ascontiguousarray(inputs[n]) for n in IN_NAMES}
    arrays["constants"] = constants()
    arrays["pos_row"], arrays["pos_col"] = position_tables()
    arrays["dft_feat"], arrays["dft_tok"] = dft_tables()
    A = {n: nc.dram_tensor(n, list(a.shape), F32, kind="ExternalInput").ap() for n, a in arrays.items()}
    outs = [nc.dram_tensor(n, list(s), F32, kind="ExternalOutput").ap() for n, s in (
        ("y_prompt", (1, PROMPT, D)), ("y_sample", (1, SAMPLE, D)), ("new_state_gla", (1, 1, 2, HEADS, DK, DK)))]
    build(nc, A, *outs)
    r = run_bass_kernel_spmd(nc, [arrays], core_ids=[0]).results[0]
    return r["y_prompt"], r["y_sample"], r["new_state_gla"]
```
